# Optimizing a Trainium2 kernel written in Bass

```python
import math
import jax, jax.numpy as jnp
from jax import lax
import numpy as np

D_MODEL = 1024
BATCH = 1
SEQ = 512
DEPTH = 1

HG_HEADS = 8
HG_DK = 128
HG_DV = D_MODEL // HG_HEADS
HG_KW = HG_HEADS * HG_DK
HG_VW = HG_HEADS * HG_DV
CHUNK = 64
CV_WIDTH = D_MODEL
CV_GROUPS = 8
CONV_K = 3
PROJ_WIDTHS = (HG_KW, HG_KW, HG_VW, HG_VW, CV_WIDTH, CV_WIDTH, CV_WIDTH, D_MODEL, D_MODEL)
PROJ_W = sum(PROJ_WIDTHS)
SPLIT_IDX = tuple(int(v) for v in np.cumsum(PROJ_WIDTHS)[:-1])
N_KEYS = 128
N_EXPERTS = N_KEYS * N_KEYS
PK_HEADS = 8
PK_DKEY = 256
PK_HALF = PK_DKEY // 2
PK_TOPK = 16
PEER_BLOCK = 128
PLE_DIM = 256
LN_EPS = 1e-5
RMS_EPS = 1e-6
ALPHA = (2.0 * DEPTH) ** 0.25
BETA = (8.0 * DEPTH) ** -0.25

kernel_name = "hybrid_hgrn2_shortconv_peer_deepnorm"

def layer_norm(x, g, b):
    xf = x.astype(jnp.float32)
    mu = jnp.mean(xf, axis=-1, keepdims=True)
    xc = xf - mu
    var = jnp.mean(xc * xc, axis=-1, keepdims=True)
    return (xc * lax.rsqrt(var + LN_EPS) * g.astype(jnp.float32) + b.astype(jnp.float32)).astype(x.dtype)

def hgrn2_chunkwise(q, k, v, logf):
    bsz, seq = q.shape[0], q.shape[1]
    n = seq // CHUNK

    def to_chunks(t):
        return t.astype(jnp.float32).reshape(bsz, n, CHUNK, HG_HEADS, t.shape[-1]).transpose(0, 3, 1, 2, 4)

    q, k, v, logf = to_chunks(q), to_chunks(k), to_chunks(v), to_chunks(logf)
    bcum = jnp.cumsum(logf, axis=3)
    qe = q * jnp.exp(bcum)
    ke = k * jnp.exp(-bcum)
    causal = jnp.tril(jnp.ones((CHUNK, CHUNK), dtype=bool))
    a = jnp.einsum('bhnik,bhnjk->bhnij', qe, ke)
    a = jnp.where(causal, a, 0.0)
    o_intra = jnp.einsum('bhnij,bhnjv->bhniv', a, v)
    b_last = bcum[:, :, :, -1:, :]
    k_end = k * jnp.exp(b_last - bcum)
    ds = jnp.einsum('bhnck,bhncv->bhnkv', k_end, v)
    decay = jnp.exp(b_last[:, :, :, 0, :])

    def step(state, inp):
        d, dsn = inp
        return d[..., None] * state + dsn, state

    s0 = jnp.zeros((bsz, HG_HEADS, HG_DK, HG_DV), jnp.float32)
    _, s_prev = lax.scan(step, s0, (jnp.moveaxis(decay, 2, 0), jnp.moveaxis(ds, 2, 0)))
    s_prev = jnp.moveaxis(s_prev, 0, 2)
    o_inter = jnp.einsum('bhnck,bhnkv->bhncv', qe, s_prev)
    o = o_intra + o_inter
    return o.transpose(0, 2, 3, 1, 4).reshape(bsz, seq, HG_HEADS, HG_DV)

def causal_depthwise_conv3(u, w, b):
    seq = u.shape[1]
    up = jnp.pad(u, ((0, 0), (CONV_K - 1, 0), (0, 0)))
    y = b
    for j in range(CONV_K):
        y = y + up[:, j:j + seq, :] * w[j]
    return y

def token_mixer(x, w_in, lb, hg_norm_g, conv_w, conv_b, w_branch_a, w_branch_b, w_out):
    bsz, seq = x.shape[0], x.shape[1]
    z = x @ w_in
    q, fz, iv, og, cb, cc, ch, ga, gb = jnp.split(z, SPLIT_IDX, axis=-1)
    q = q.reshape(bsz, seq, HG_HEADS, HG_DK) * (HG_DK ** -0.5)
    fz = fz.reshape(bsz, seq, HG_HEADS, HG_DK).astype(jnp.float32)
    lbh = lb.reshape(HG_HEADS, HG_DK)
    f = lbh + (1.0 - lbh) * jax.nn.sigmoid(fz)
    logf = jnp.log(f)
    kin = (1.0 - lbh) * jax.nn.sigmoid(-fz)
    v = iv.reshape(bsz, seq, HG_HEADS, HG_DV)
    o = hgrn2_chunkwise(q, kin, v, logf)
    o = o * lax.rsqrt(jnp.mean(o * o, axis=-1, keepdims=True) + RMS_EPS)
    o = o * hg_norm_g.reshape(HG_HEADS, HG_DV).astype(jnp.float32)
    o = o.reshape(bsz, seq, HG_VW).astype(x.dtype) * jax.nn.silu(og)
    yc = cb * causal_depthwise_conv3(cc * ch, conv_w, conv_b)
    merged = jax.nn.sigmoid(ga) * (o @ w_branch_a) + jax.nn.sigmoid(gb) * (yc @ w_branch_b)
    return merged @ w_out

def peer(x, w_q, sub_keys, u, v):
    bsz, seq, d = x.shape
    xt = x.reshape((bsz * seq) // PEER_BLOCK, PEER_BLOCK, d)

    def block(xb):
        tb = xb.shape[0]
        qh = (xb @ w_q).reshape(tb, PK_HEADS, 2, PK_HALF)
        s = jnp.einsum('thpd,hpkd->thpk', qh, sub_keys).astype(jnp.float32)
        s1, i1 = lax.top_k(s[:, :, 0], PK_TOPK)
        s2, i2 = lax.top_k(s[:, :, 1], PK_TOPK)
        cand = (s1[..., :, None] + s2[..., None, :]).reshape(tb, PK_HEADS, PK_TOPK * PK_TOPK)
        cidx = (i1[..., :, None] * N_KEYS + i2[..., None, :]).reshape(tb, PK_HEADS, PK_TOPK * PK_TOPK)
        top, pos = lax.top_k(cand, PK_TOPK)
        eidx = jnp.take_along_axis(cidx, pos, axis=-1)
        g = jax.nn.softmax(top, axis=-1).astype(xb.dtype)
        ue = jnp.take(u, eidx, axis=0)
        h = jax.nn.gelu(jnp.einsum('thkd,td->thk', ue, xb), approximate=False)
        ve = jnp.take(v, eidx, axis=0)
        return jnp.einsum('thk,thkd->td', g * h, ve)

    out = lax.map(block, xt)
    return out.reshape(bsz, seq, d)

def setup_inputs(seed: int = 0) -> dict:
    key = jax.random.key(seed)
    ks = jax.random.split(key, 20)
    f32 = jnp.float32
    nrm = lambda k, shape, s: jax.random.normal(k, shape, f32) * s
    return {
        "x": nrm(ks[0], (BATCH, SEQ, D_MODEL), 1.0),
        "p": nrm(ks[1], (DEPTH, BATCH, SEQ, PLE_DIM), 1.0),
        "w_in": nrm(ks[2], (DEPTH, D_MODEL, PROJ_W), D_MODEL ** -0.5),
        "lb_param": nrm(ks[3], (DEPTH + 1, HG_KW), 0.5),
        "hg_norm_g": 1.0 + nrm(ks[4], (DEPTH, HG_VW), 0.02),
        "conv_w": nrm(ks[5], (DEPTH, CONV_K, CV_WIDTH), CONV_K ** -0.5),
        "conv_b": nrm(ks[6], (DEPTH, CV_WIDTH), 0.02),
        "w_branch_a": nrm(ks[7], (DEPTH, HG_VW, D_MODEL), BETA * HG_VW ** -0.5),
        "w_branch_b": nrm(ks[8], (DEPTH, CV_WIDTH, D_MODEL), BETA * CV_WIDTH ** -0.5),
        "w_out": nrm(ks[9], (DEPTH, D_MODEL, D_MODEL), BETA * D_MODEL ** -0.5),
        "ln1_g": 1.0 + nrm(ks[10], (DEPTH, D_MODEL), 0.02),
        "ln1_b": nrm(ks[11], (DEPTH, D_MODEL), 0.02),
        "pk_w_q": nrm(ks[12], (DEPTH, D_MODEL, PK_HEADS * PK_DKEY), D_MODEL ** -0.5),
        "pk_sub_keys": nrm(ks[13], (DEPTH, PK_HEADS, 2, N_KEYS, PK_HALF), PK_HALF ** -0.5),
        "pk_u": nrm(ks[14], (DEPTH, N_EXPERTS, D_MODEL), D_MODEL ** -0.5),
        "pk_v": nrm(ks[15], (DEPTH, N_EXPERTS, D_MODEL), BETA),
        "ln2_g": 1.0 + nrm(ks[16], (DEPTH, D_MODEL), 0.02),
        "ln2_b": nrm(ks[17], (DEPTH, D_MODEL), 0.02),
        "ple_w_gate": nrm(ks[18], (DEPTH, D_MODEL, D_MODEL), D_MODEL ** -0.5),
        "ple_w_proj": nrm(ks[19], (DEPTH, PLE_DIM, D_MODEL), PLE_DIM ** -0.5),
    }

def reference(x, p, w_in, lb_param, hg_norm_g, conv_w, conv_b, w_branch_a, w_branch_b, w_out,
              ln1_g, ln1_b, pk_w_q, pk_sub_keys, pk_u, pk_v, ln2_g, ln2_b, ple_w_gate, ple_w_proj):
    lb_all = jnp.cumsum(jax.nn.softmax(lb_param.astype(jnp.float32), axis=0), axis=0)
    for i in range(DEPTH):
        mix = token_mixer(x, w_in[i], lb_all[i], hg_norm_g[i], conv_w[i], conv_b[i],
                          w_branch_a[i], w_branch_b[i], w_out[i])
        x = layer_norm(ALPHA * x + mix, ln1_g[i], ln1_b[i])
        x = layer_norm(ALPHA * x + peer(x, pk_w_q[i], pk_sub_keys[i], pk_u[i], pk_v[i]), ln2_g[i], ln2_b[i])
        x = x + jax.nn.sigmoid(x @ ple_w_gate[i]) * (p[i] @ ple_w_proj[i])
    return x


_drawn_inputs = setup_inputs


def setup_inputs(seed=0):
    import zlib

    import numpy as np

    out = dict(_drawn_inputs(seed))
    spreads = {}
    factors = {'hg_norm_g': 5.348, 'conv_b': 4.018, 'ln2_g': 3.176, 'ln2_b': 3.194}
    for name, (base, spread) in spreads.items():
        noise = np.random.default_rng([zlib.crc32(name.encode()), seed]).standard_normal(out[name].shape)
        drawn = base * np.exp(spread * noise) if base else spread * noise
        out[name] = __import__('jax').numpy.asarray(drawn.astype(out[name].dtype))
    for name, factor in factors.items():
        out[name] = (out[name] * factor).astype(out[name].dtype)
    return out
```

```python
from contextlib import ExitStack

import concourse.bass as bass
import numpy as np
from concourse import mybir

P = 128
F32 = mybir.dt.float32
F32R = mybir.dt.float32r
U32 = mybir.dt.uint32
ALU = mybir.AluOpType
ACT = mybir.ActivationFunctionType
AX_X = mybir.AxisListType.X


def build(nc, x, p, w_in, lb_param, hg_norm_g, conv_w, conv_b, w_branch_a, w_branch_b, w_out,
          ln1_g, ln1_b, pk_w_q, pk_sub_keys, pk_u, pk_v, ln2_g, ln2_b, ple_w_gate, ple_w_proj, out):
    SEQ, D = x.shape[1], x.shape[2]
    TB = SEQ // P
    KT = D // P
    HEADS = lb_param.shape[1] // P
    CH = 64
    NCH = SEQ // CH
    PKH = pk_sub_keys.shape[1]
    NK = pk_sub_keys.shape[3]
    TOPK = 16
    ALPHA = 2.0 ** 0.25
    LN_EPS, RMS_EPS = 1e-5, 1e-6
    CW = 2 * P
    PLE = p.shape[3]
    UR, VR, DR = 8, 4, 4
    ITEMS = TB * PKH
    PIECES = [(0, 1), (1, TB)]

    xf = x.rearrange("a (b p) d -> p (a b) d", p=P)
    w_in_v = w_in[0].rearrange("(k p) n -> p k n", p=P)

    ctx = ExitStack()
    with ctx:
        K = 1024
        at = nc.sbuf_base + (-nc.sbuf_base) % 64

        def place(name, shape, dt, offset):
            return nc.alloc_sbuf_tensor_at(name, [P] + shape, dt, offset=offset)

        o_x = at
        o_mix = o_x + 16 * K
        o_xt = o_mix + 64 * K
        o_raw = o_xt + 32 * K
        o_ring = o_raw + 32 * K
        o_ln = o_ring + 48 * K
        o_misc = o_ln + 8 * K

        x_sb = place("x_sb", [TB, D], F32, o_x)
        oT = place("oT", [KT, SEQ], F32, o_mix)
        ycT = place("ycT", [KT, SEQ], F32, o_mix + 16 * K)
        gaT = place("gaT", [KT, SEQ], F32, o_mix + 32 * K)
        gbT = place("gbT", [KT, SEQ], F32, o_mix + 48 * K)
        xTh = place("xTh", [KT, SEQ], F32R, o_xt)
        xTl = place("xTl", [KT, SEQ], F32R, o_xt + 16 * K)
        raw = place("raw", [4, KT, CW], F32, o_raw)
        w_hi = place("w_hi", [2, KT, P], F32R, o_ring)
        w_lo = place("w_lo", [2, KT, P], F32R, o_ring + 8 * K)

        def scratch(name, shape, offset, dt=F32):
            return place(name, shape, dt, offset)

        e_pos = scratch("e_pos", [2, SEQ], o_mix + 32 * K)
        qe = scratch("qe", [2, SEQ], o_mix + 36 * K)
        ke = scratch("ke", [2, SEQ], o_mix + 40 * K)
        kend = scratch("kend", [2, SEQ], o_mix + 44 * K)
        og_silu = scratch("og_silu", [2, SEQ], o_mix + 48 * K)
        vT_sb = scratch("vT_sb", [SEQ], o_mix + 52 * K)
        v_tok = scratch("v_tok", [TB, P], o_mix + 54 * K)
        k_even = scratch("k_even", [TB, P], o_mix + 56 * K)
        k_odd = scratch("k_odd", [TB, P], o_mix + 58 * K)
        att = scratch("att", [TB, P], o_mix + 60 * K)
        o_sq = scratch("o_sq", [SEQ], o_mix + 62 * K)
        rms_ln = scratch("rms_ln", [SEQ], o_ln)
        rms_r = scratch("rms_r", [SEQ], o_ln + 2 * K)
        state = scratch("state", [NCH - 1, P], o_ln + 4 * K)
        z0 = o_ring + 16 * K
        sg_pos = scratch("sg_pos", [SEQ], z0)
        sg_neg = scratch("sg_neg", [SEQ], z0 + 2 * K)
        log_f = scratch("log_f", [SEQ], z0 + 4 * K)
        bcum = scratch("bcum", [SEQ], z0 + 6 * K)
        tail_e = scratch("tail_e", [SEQ], z0 + 8 * K)
        e_neg = scratch("e_neg", [SEQ], z0 + 10 * K)
        sg_og = scratch("sg_og", [SEQ], z0 + 12 * K)
        o_norm = scratch("o_norm", [SEQ], z0 + 14 * K)
        chunk_mask = scratch("chunk_mask", [SEQ], z0 + 16 * K)
        ch_sb = scratch("ch_sb", [SEQ], z0 + 18 * K)
        u_pad = scratch("u_pad", [SEQ + 2], z0 + 20 * K)
        y_a = scratch("y_a", [SEQ], z0 + 23 * K)
        y_b = scratch("y_b", [SEQ], z0 + 25 * K)
        vec_rows = scratch("vec_rows", [P], z0 + 27 * K)
        causal = scratch("causal", [P], z0 + 28 * K)
        ones = scratch("ones", [P], z0 + 29 * K)

        misc = [o_misc]

        def small(name, shape, dt=F32):
            t = place(name, shape, dt, misc[0])
            misc[0] += -(-int(np.prod(shape)) * 4 // 32) * 32
            return t

        ident = small("ident", [P])
        NV = 2 * HEADS + HEADS + 3 * KT + KT
        vecs = small("vecs", [NV])
        lb_m = small("lb_m", [HEADS])
        lb_e = small("lb_e", [2, HEADS])
        lb = small("lb", [HEADS])
        one_lb = small("one_lb", [HEADS])
        lb0, lb1 = vecs[:, 0:HEADS], vecs[:, HEADS:2 * HEADS]
        scores = place("scores", [TB, PKH, 2, NK], F32, o_xt)
        keysT = place("keysT", [PKH * 2, NK], F32, o_raw + 3 * 8 * K)
        u_ring = place("u_ring", [UR, D], F32, o_ring)
        v_ring = place("v_ring", [VR, D], F32, o_ring + UR * 4 * K)
        qhT = [place("qhT0", [2, P], F32, o_xt + 31 * K), place("qhT1", [2, SEQ - P], F32, o_mix + 16 * K)]
        ln1 = place("ln1", [2, D], F32, o_ln)
        w_ple = place("w_ple", [PLE // P, D], F32, o_mix)
        ln2 = place("ln2", [2, D], F32, o_mix + 8 * K)
        x2 = place("x2", [D], F32, o_mix + 16 * K)
        x2T = place("x2T", [KT, P], F32, o_mix + 20 * K)
        gate = place("gate", [D], F32, o_mix + 24 * K)
        pT = place("pT", [PLE // P, P], F32, o_mix + 28 * K)
        p_sb = place("p_sb", [PLE], F32, o_mix + 29 * K)
        acc = place("acc", [D], F32, o_mix + 24 * K)
        w_gate = place("w_gate", [KT, D], F32, o_mix + 32 * K)

        stage = small("stage", [2, NK])
        cand = small("cand", [TOPK * TOPK])
        hot = small("hot", [TOPK * TOPK])
        best = small("best", [2, TOPK])
        best_i = small("best_i", [2, TOPK], U32)
        top = small("top", [TOPK])
        pos = small("pos", [TOPK], U32)
        pos_hi, pos_lo = small("pos_hi", [TOPK], U32), small("pos_lo", [TOPK], U32)
        sel = small("sel", [2, TOPK])
        idx = small("idx", [2, TOPK], U32)
        idx_v = small("idx_v", [2, TOPK], U32)
        top_e = small("top_e", [TOPK])
        e_sum, e_rec = small("e_sum", [1]), small("e_rec", [1])
        weight = small("weight", [2, TOPK])
        dots = small("dots", [2, TOPK])
        gelu = small("gelu", [TOPK])
        coef = small("coef", [TOPK])
        iota16 = small("iota16", [TOPK])
        diag = small("diag", [DR, P])
        stats = small("stats", [2, 6])
        mean_var = small("mean_var", [2])
        rstd = small("rstd", [2])
        eps_rms = small("eps_rms", [1])
        eps_ln = small("eps_ln", [1])

        psum = ctx.enter_context(nc.psum_tensor("psum", [P, 8, 512], F32))
        B = [psum[:, i, :] for i in range(8)]
        x_cur = psum[:, 2:4, :].rearrange("p a d -> p (a d)")

        def sem(name):
            return ctx.enter_context(nc.semaphore(name))

        x_in = [sem(f"x_in{b}") for b in range(TB)]
        vecs_in = sem("vecs_in")
        raw_in = [sem(f"raw_in{i}") for i in range(4)]
        consts = sem("consts")
        vec_t = sem("vec_t")
        lb_step = sem("lb_step")
        x_tr, xh_done, xl_done = sem("x_tr"), sem("xh_done"), sem("xl_done")
        hi_done, lo_done, unit_done = sem("hi_done"), sem("lo_done"), sem("unit_done")
        f_sig, lnf_done, cum_done = sem("f_sig"), sem("lnf_done"), sem("cum_done")
        ep_done, en_done, dif_done, et_done = sem("ep_done"), sem("en_done"), sem("dif_done"), sem("et_done")
        qe_done, ke_done, kend_done = sem("qe_done"), sem("ke_done"), sem("kend_done")
        vT_done, sgo_done, ogs_done = sem("vT_done"), sem("sgo_done"), sem("ogs_done")
        vtr_done, ktr_done, a_done = sem("vtr_done"), sem("ktr_done"), sem("a_done")
        vtok_done, ktok_done, att_done = sem("vtok_done"), sem("ktok_done"), sem("att_done")
        ds_done, st_done, o_done = sem("ds_done"), sem("st_done"), sem("o_done")
        sq_done, rms_done, rln_done, rr_done = sem("sq_done"), sem("rms_done"), sem("rln_done"), sem("rr_done")
        on_done, oT_done = sem("on_done"), sem("oT_done")
        ch_done, cv_step, yc_done, gate_done = sem("ch_done"), sem("cv_step"), sem("yc_done"), sem("gate_done")
        stored = sem("stored")
        t_done = sem("t_done")
        t_dve, t_act = sem("t_dve"), sem("t_act")
        merge_step, merged = sem("merge_step"), sem("merged")
        keys_in, keys_tr, keys_done = sem("keys_in"), sem("keys_tr"), sem("keys_done")
        ln1_in = sem("ln1_in")
        ln_step, ln_var, ln_rstd, x1_done = sem("ln_step"), sem("ln_var"), sem("ln_rstd"), sem("x1_done")
        x1_cur = sem("x1_cur")
        u_in = [sem(f"u_in{i}") for i in range(UR)]
        v_in = [sem(f"v_in{i}") for i in range(VR)]
        u_used, v_used, diag_done = sem("u_used"), sem("v_used"), sem("diag_done")
        staged, tk, exp_done, idx_done, idxv_done = sem("staged"), sem("tk"), sem("exp_done"), sem("idx_done"), sem("idxv_done")
        rec_done, weight_done, gelu_done, coef_done = sem("rec_done"), sem("weight_done"), sem("gelu_done"), sem("coef_done")
        acc_step = sem("acc_step")
        acc_out = sem("acc_out")
        fin_in, p_in = sem("fin_in"), sem("p_in")
        x2_step, x2_var, x2_rstd, x2_done = sem("x2_step"), sem("x2_var"), sem("x2_rstd"), sem("x2_done")
        x2_tr, x2T_done, p_tr, pT_done = sem("x2_tr"), sem("x2T_done"), sem("p_tr"), sem("pT_done")
        g_mm, g_sig, p_mm, fin_step, x3_done = sem("g_mm"), sem("g_sig"), sem("p_mm"), sem("fin_step"), sem("x3_done")

        block = ctx.enter_context(nc.Block())

        TK, TK_DIFF = 25, 17
        MERGE_AT = [9, 11, 13, 15] + [18 + 3 * k for k in range(12)]
        OUT_AT = [54 + 2 * k for k in range(4 * (TB - 1))]
        NORM_AT = [OUT_AT[-1] + 6 + 3 * k for k in range(TB - 1)]
        TURN_AT = [t + 4 for t in NORM_AT]
        QUERY_AT = [TURN_AT[-1] + 2 + 17 * k // 8 for k in range(2 * PKH)]
        SCORE_AT = [QUERY_AT[2 * h + 1] + 1 for h in range(PKH)]
        EVAC = 2
        LAST_ROW = TOPK * PKH - 1

        SHARED = [(g, j) for g, js in ((PKH - 3, range(1, TOPK, 2)),
                                       (PKH - 2, (1, 3, 5, 7, 8, 9, 10, 11))) for j in js]
        SHARED_ROWS = len(SHARED)

        def by_vector(g, j):
            return isinstance(g, int) and (g, j) in SHARED

        def v_row(g, j):
            if isinstance(g, int):
                return sum(not by_vector(q, r) for q in range(g + 1) for r in range(TOPK if q < g else j))
            return TOPK * g + j - SHARED_ROWS

        def diag_slot(g, j):
            return v_row(g, j) % DR if isinstance(g, int) else j % DR

        def v_reader(g, j):
            if by_vector(g, j):
                return acc_step, SHARED.index((g, j)) + 1
            return v_used, v_row(g, j) + 1

        def jobs(places, h, j, lag=0):
            return [k for k, t in enumerate(places) if min(t + lag, LAST_ROW) == TOPK * h + j]

        CONSTS = 15

        wait_regs = {}

        def wait_apart(eng, semaphore, value):
            if not isinstance(value, int):
                if eng not in wait_regs:
                    wait_regs[eng] = eng.alloc_register("wait_value")
                eng.reg_mov(wait_regs[eng], value)
                value = wait_regs[eng]
                eng.wait_ge(consts, CONSTS)
            eng.wait_ge(semaphore, value)

        Q, FZ, IV, OG, CB, CC, CHH, GA, GB = [i * D for i in range(9)]
        A_SECT = [FZ, Q, IV, OG]
        C_SECT = [CHH, CC, CB]
        G_SECT = [GA, GB]
        A_UNITS = 4 * HEADS
        C_UNITS = 3 * KT
        G_SLOT = [3, 0]

        def unit_a(h, j):
            return 4 * h + j

        def unit_c(c, j):
            return A_UNITS + 3 * c + j

        def unit_g(c, j):
            return A_UNITS + C_UNITS + 2 * c + j

        T_CHUNKS = 4 + 4 + 4 + PKH
        RAW_LOADS = [3 * (KT // 2), 2 * (KT // 2), 2 * (KT // 2)]

        def t_chunk(pc, m):
            n = T_CHUNKS * pc + m
            slot = (n + 1) % 3
            return n, slot, RAW_LOADS[slot] + n // 3 + 1

        def blocks(pc):
            return range(*PIECES[pc])

        def t_base(pc):
            return sum(16 + 6 * len(blocks(q)) + 4 * PKH for q in range(pc))

        def use_merge(pc, c, i):
            return t_base(pc) + 4 * c + i

        def use_out(pc, c, b):
            return t_base(pc) + 16 + len(blocks(pc)) * c + b - blocks(pc)[0]

        def use_turn(pc, b, kh):
            return t_base(pc) + 16 + 4 * len(blocks(pc)) + 2 * (b - blocks(pc)[0]) + kh

        def use_query(pc, h, i):
            return t_base(pc) + 16 + 6 * len(blocks(pc)) + 4 * h + i

        def chunk_end(n):
            pc, m = divmod(n, T_CHUNKS)
            if m < 8:
                return use_merge(pc, m // 2, 2 * (m % 2) + 1) + 1
            if m < 12:
                return use_out(pc, m - 8, blocks(pc)[-1]) + 1
            return use_query(pc, m - 12, 1) + 1

        def t_reader(r):
            pc = 0 if r < t_base(1) else 1
            n_dve, n_act = 16 + 4 * len(blocks(pc)), 2 * len(blocks(pc)) + 4 * PKH
            before_dve = sum(16 + 4 * len(blocks(q)) for q in range(pc))
            before_act = sum(2 * len(blocks(q)) + 4 * PKH for q in range(pc))
            i = r - t_base(pc)
            return (t_dve, before_dve + i + 1) if i < n_dve else (t_act, before_act + i - n_dve + 1)

        @block.sync
        def _(sp):
            rows = 0
            for src, n in ((lb_param.rearrange("a (h k) -> (a h) k", k=P), 2 * HEADS),
                           (hg_norm_g.rearrange("a (h k) -> (a h) k", k=P), HEADS),
                           (conv_w[0].rearrange("j (c k) -> (j c) k", k=P), 3 * KT),
                           (conv_b.rearrange("a (c k) -> (a c) k", k=P), KT)):
                sp.dma_start(vec_rows[rows:rows + n, :], src).then_inc(vecs_in, 16)
                rows += n
            for b in range(TB):
                sp.dma_start(x_sb[:, b, :], xf[:, b, :]).then_inc(x_in[b], 16)

            def load(slot, col):
                sp.dma_start(raw[:, slot], w_in_v[:, :, bass.ds(col, CW)]).then_inc(raw_in[slot], 16)

            for j in range(4):
                load(j, A_SECT[j])
            with sp.Fori(1, HEADS // 2) as hp:
                for j in range(4):
                    wait_apart(sp, lo_done, 8 * hp - 8 + 5 + j)
                    load(j, A_SECT[j] + hp * CW)
            for j in range(3):
                sp.wait_ge(lo_done, unit_a(HEADS - 1, j) + 1)
                load(j, C_SECT[j])
            sp.wait_ge(lo_done, unit_a(HEADS - 1, 3) + 1)
            load(G_SLOT[0], GA)
            with sp.Fori(1, KT // 2) as cp:
                for j in range(3):
                    wait_apart(sp, lo_done, 6 * cp - 6 + A_UNITS + 3 + j + 1)
                    load(j, C_SECT[j] + cp * CW)
            sp.wait_ge(lo_done, unit_c(KT - 1, 0) + 1)
            load(G_SLOT[1], GB)
            with sp.Fori(1, KT // 2) as cp:
                for j in range(2):
                    wait_apart(sp, lo_done, 4 * cp - 4 + A_UNITS + C_UNITS + 2 + j + 1)
                    load(G_SLOT[j], G_SECT[j] + cp * CW)

            def tail_load(pc, m, w, col):
                n, slot, _ = t_chunk(pc, m)
                if n < 3:
                    sp.wait_ge(lo_done, (unit_g(KT - 1, 1), unit_c(KT - 1, 1), unit_c(KT - 1, 2))[slot] + 1)
                else:
                    sp.wait_ge(t_done, chunk_end(n - 3))
                sp.dma_start(raw[:, slot], w.rearrange("(k p) n -> p k n", p=P)[:, :, col:col + CW]).then_inc(
                    raw_in[slot], 16)

            def tail_loads(pc):
                for c in range(4):
                    tail_load(pc, 2 * c, w_branch_a[0], c * CW)
                    tail_load(pc, 2 * c + 1, w_branch_b[0], c * CW)
                    if pc == 0 and c == 0:
                        sp.wait_ge(oT_done, HEADS)
                        for i, g in enumerate((ln1_g, ln1_b)):
                            sp.dma_start(ln1[:, i, :], g[0].partition_broadcast(P)).then_inc(ln1_in, 16)
                        sp.wait_ge(lo_done, unit_g(KT - 1, 0) + 1)
                        sp.dma_start(keysT[:], pk_sub_keys[0].rearrange("h s k d -> k (h s) d")).then_inc(keys_in, 16)
                for c in range(4):
                    tail_load(pc, 8 + c, w_out[0], c * CW)
                for h in range(PKH):
                    tail_load(pc, 12 + h, pk_w_q[0], h * CW)

            tail_loads(0)
            tail_loads(1)
            sp.wait_ge(t_done, use_query(1, 0, 0))
            sp.dma_start(w_gate[:], ple_w_gate[0].rearrange("(k p) n -> p k n", p=P)).then_inc(fin_in, 16)
            sp.wait_ge(t_done, t_base(2))
            sp.wait_ge(*t_reader(t_base(2) - 1))
            sp.dma_start(w_ple[:], ple_w_proj[0].rearrange("(k p) n -> p k n", p=P)).then_inc(fin_in, 16)
            for i, g in enumerate((ln2_g, ln2_b)):
                sp.dma_start(ln2[:, i, :], g[0].partition_broadcast(P)).then_inc(fin_in, 16)

            pv = p[0].rearrange("a (b p) d -> p (a b) d", p=P)
            ov = out.rearrange("a (b p) d -> p (a b) d", p=P)

            def store(b):
                sp.wait_ge(x3_done, b + 1)
                sp.dma_start(ov[:, bass.ds(b, 1), :].rearrange("p a d -> p (a d)"), x2[:]).then_inc(stored, 16)

            def load_p(b):
                sp.dma_start(p_sb[:], pv[:, bass.ds(b, 1), :].rearrange("p a d -> p (a d)")).then_inc(p_in, 16)

            load_p(0)
            with sp.Fori(0, TB - 1) as b:
                store(b)
                load_p(b + 1)
            store(TB - 1)
            sp.wait_ge(stored, 16 * TB)

        @block.gpsimd
        def _(pool):
            pool.memset(ident[:], 0.0).then_inc(consts, 1)
            pool.memset(causal[:], 1.0).then_inc(consts, 1)
            pool.memset(ones[:], 1.0 / P).then_inc(consts, 1)
            pool.memset(chunk_mask[:], 1.0).then_inc(consts, 1)
            pool.memset(u_pad[:, 0:2], 0.0).then_inc(consts, 1)
            pool.memset(k_even[:], 0.0).then_inc(consts, 1)
            pool.memset(k_odd[:], 0.0).then_inc(consts, 1)
            pool.memset(att[:], 0.0).then_inc(consts, 1)
            pool.memset(eps_rms[:], RMS_EPS).then_inc(consts, 1)
            pool.memset(eps_ln[:], LN_EPS).then_inc(consts, 1)
            pool.wait_ge(consts, 10)
            pool.affine_select(out=ident[:], in_=ident[:], compare_op=ALU.not_equal, fill=1.0, base=0,
                               pattern=[[-1, P]], channel_multiplier=1).then_inc(consts, 1)
            pool.affine_select(out=causal[:], in_=causal[:], compare_op=ALU.is_ge, fill=0.0, base=0,
                               pattern=[[1, P]], channel_multiplier=-1).then_inc(consts, 1)
            pool.memset(chunk_mask[:].rearrange("p (c t) -> p c t", t=CH)[:, :, 0:1], 0.0).then_inc(consts, 1)
            pool.wait_ge(consts, 13)
            pool.memset(causal[0:CH, CH:P], 0.0).then_inc(consts, 1)
            pool.iota(iota16[:], [[1, TOPK]], base=0, channel_multiplier=0,
                      allow_small_or_imprecise_dtypes=True).then_inc(consts, 1)

            u_rows, v_rows = pk_u[0], pk_v[0]

            def gather_u(i, s, j):
                if not (isinstance(i, int) and 16 * i + j < UR):
                    wait_apart(pool, u_used, TOPK * i + j - UR + 1)
                pool.indirect_dma_start(u_ring[:, j % UR, :], None, u_rows,
                                        bass.IndirectOffsetOnAxis(idx[:, s, j:j + 1], 0)).then_inc(u_in[j % UR], 16)

            def gather_v(g, s, j):
                if not (isinstance(g, int) and TOPK * g + j < VR):
                    before = divmod(TOPK * g + j - VR, TOPK) if isinstance(g, int) else (g, j - VR)
                    wait_apart(pool, *v_reader(*before))
                pool.indirect_dma_start(v_ring[:, j % VR, :], None, v_rows,
                                        bass.IndirectOffsetOnAxis(idx_v[:, s, j:j + 1], 0)).then_inc(v_in[j % VR], 16)

            def keep_idx(g, s):
                pool.tensor_copy(idx_v[:, s, :], idx[:, s, :]).then_inc(idxv_done, 1)
                wait_apart(pool, idxv_done, g + 1)

            def item(i, s):
                first = isinstance(i, int) and i == 0
                wait_apart(pool, idx_done, i + 1)
                if not first:
                    keep_idx(i - 1, 1 - s)
                for j in range(TOPK):
                    gather_u(i, s, j)
                    if not first:
                        gather_v(i - 1, 1 - s, j)

            pool.wait_ge(keys_done, 4)
            for h in range(PKH):
                item(h, h % 2)
            with pool.Fori(PKH // 2, ITEMS // 2) as ip:
                item(2 * ip, 0)
                item(2 * ip + 1, 1)
            keep_idx(ITEMS - 1, 1)
            for j in range(TOPK):
                gather_v(ITEMS - 1, 1, j)

        @block.scalar
        def _(act):
            act.wait_ge(lb_step, 3)
            nc.scalar.activation(lb_e[:].rearrange("p a h -> p (a h)"), lb_e[:].rearrange("p a h -> p (a h)"),
                                 ACT.Exp).then_inc(lb_step, 1)
            def hi(n, s, kind_slot, half, loads):
                act.wait_ge(raw_in[kind_slot], 16 * loads)
                if not (isinstance(n, int) and n < 2):
                    act.wait_ge(unit_done, n - 1)
                nc.scalar.activation(w_hi[:, s], raw[:, kind_slot, :, half * P:half * P + P],
                                     ACT.Copy).then_inc(hi_done, 1)

            def rms_tail(h):
                act.wait_ge(rms_done, h + 1)
                if not (isinstance(h, int) and h < 1):
                    act.wait_ge(oT_done, h)
                nc.scalar.activation(rms_ln[:], B[4][:], ACT.Ln, bias=eps_rms[:, 0:1]).then_inc(rln_done, 1)
                act.wait_ge(rln_done, h + 1)
                nc.scalar.activation(rms_r[:], rms_ln[:], ACT.Exp, scale=-0.5).then_inc(rr_done, 1)

            def og_sigmoid(h):
                act.wait_ge(unit_done, unit_a(h, 3) + 1)
                if not (isinstance(h, int) and h < 1):
                    act.wait_ge(ogs_done, h)
                nc.scalar.activation(sg_og[:], B[3][:], ACT.Sigmoid).then_inc(sgo_done, 1)

            def forget(h):
                act.wait_ge(unit_done, unit_a(h, 0) + 1)
                if not (isinstance(h, int) and h < 1):
                    act.wait_ge(kend_done, h)
                nc.scalar.activation(sg_pos[:], B[0][:], ACT.Sigmoid).then_inc(f_sig, 1)
                nc.scalar.activation(sg_neg[:], B[0][:], ACT.Sigmoid, scale=-1.0).then_inc(f_sig, 1)

            def tokens_out(g):
                act.wait_ge(vtr_done, g + 1)
                nc.scalar.activation(v_tok[:].rearrange("p b v -> p (b v)"), B[6][:], ACT.Copy).then_inc(vtok_done, 1)
                act.wait_ge(ktr_done, g + 1)
                nc.scalar.activation(k_even[0:CH].rearrange("p b v -> p (b v)"), B[7][0:CH, :],
                                     ACT.Copy).then_inc(ktok_done, 1)
                nc.scalar.activation(k_odd[CH:P].rearrange("p b v -> p (b v)"), B[7][CH:P, :],
                                     ACT.Copy).then_inc(ktok_done, 1)

            def exps(h, s):
                act.wait_ge(f_sig, 2 * h + 2)
                nc.scalar.activation(log_f[:], sg_pos[:], ACT.Ln, bias=lb[:, bass.ds(h, 1)],
                                     scale=one_lb[:, bass.ds(h, 1)]).then_inc(lnf_done, 1)
                act.wait_ge(cum_done, h + 1)
                nc.scalar.activation(e_pos[:, s], bcum[:], ACT.Exp).then_inc(ep_done, 1)
                nc.scalar.activation(e_neg[:], bcum[:], ACT.Exp, scale=-1.0).then_inc(en_done, 1)
                act.wait_ge(dif_done, h + 1)
                nc.scalar.activation(tail_e[:], tail_e[:], ACT.Exp, scale=-1.0).then_inc(et_done, 1)

            def v_out(h):
                act.wait_ge(unit_done, unit_a(h, 2) + 1)
                nc.scalar.activation(vT_sb[:], B[2][:], ACT.Copy).then_inc(vT_done, 1)

            def square(g):
                act.wait_ge(o_done, g + 1)
                nc.scalar.activation(o_sq[:], B[5][:], ACT.Square).then_inc(sq_done, 1)

            def a_loads(h):
                return (h // 2 + 1) if isinstance(h, int) else None

            def head(h, s, loads, next_hi):
                first = isinstance(h, int)
                hi(unit_a(h, 1), 1, 1, s, loads)
                if not (first and h < 2):
                    rms_tail(h - 2)
                if not (first and h < 1):
                    og_sigmoid(h - 1)
                forget(h)
                if not (first and h < 1):
                    tokens_out(h - 1)
                hi(unit_a(h, 2), 0, 2, s, loads)
                exps(h, s)
                hi(unit_a(h, 3), 1, 3, s, loads)
                v_out(h)
                next_hi()
                if not (first and h < 1):
                    square(h - 1)

            for k in range(KT):
                act.wait_ge(x_tr, k + 1)
                nc.scalar.activation(xTh[:, k, :], B[k][:], ACT.Copy).then_inc(xh_done, 1)
                if k == KT // 2 - 1:
                    hi(0, 0, 0, 0, 1)
            act.wait_ge(lb_step, 7)
            head(0, 0, 1, lambda: hi(unit_a(1, 0), 0, 0, 1, 1))
            head(1, 1, 1, lambda: hi(unit_a(2, 0), 0, 0, 0, 2))
            with act.Fori(1, HEADS // 2 - 1) as hp:
                head(2 * hp, 0, hp + 1, lambda: hi(unit_a(2 * hp + 1, 0), 0, 0, 1, hp + 1))
                head(2 * hp + 1, 1, hp + 1, lambda: hi(unit_a(2 * hp + 2, 0), 0, 0, 0, hp + 2))
            L = HEADS // 2
            head(HEADS - 2, 0, L, lambda: hi(unit_a(HEADS - 1, 0), 0, 0, 1, L))
            head(HEADS - 1, 1, L, lambda: hi(unit_c(0, 0), 0, 0, 0, L + 1))

            def conv_tile(c, s, loads, next_hi):
                u0 = s
                hi(unit_c(c, 1), (u0 + 1) % 2, 1, s, loads)
                if isinstance(c, int) and c == 0:
                    rms_tail(HEADS - 2)
                    og_sigmoid(HEADS - 1)
                    tokens_out(HEADS - 1)
                act.wait_ge(unit_done, unit_c(c, 0) + 1)
                if not (isinstance(c, int) and c == 0):
                    act.wait_ge(cv_step, 4 * c)
                nc.scalar.activation(ch_sb[:], B[0][:], ACT.Copy).then_inc(ch_done, 1)
                hi(unit_c(c, 2), u0, 2, s, loads)
                next_hi()
                if isinstance(c, int) and c == 0:
                    square(HEADS - 1)
                if isinstance(c, int) and c == 1:
                    rms_tail(HEADS - 1)

            C = KT // 2
            conv_tile(0, 0, L + 1, lambda: hi(unit_c(1, 0), 1, 0, 1, L + 1))
            conv_tile(1, 1, L + 1, lambda: hi(unit_c(2, 0), 0, 0, 0, L + 2))
            with act.Fori(1, C - 1) as cp:
                conv_tile(2 * cp, 0, cp + L + 1, lambda: hi(unit_c(2 * cp + 1, 0), 1, 0, 1, cp + L + 1))
                conv_tile(2 * cp + 1, 1, cp + L + 1, lambda: hi(unit_c(2 * cp + 2, 0), 0, 0, 0, cp + L + 2))
            conv_tile(KT - 2, 0, L + C, lambda: hi(unit_c(KT - 1, 0), 1, 0, 1, L + C))
            conv_tile(KT - 1, 1, L + C, lambda: hi(unit_g(0, 0), 0, G_SLOT[0], 0, L + 1))

            def gate_out(c, j):
                act.wait_ge(unit_done, unit_g(c, j) + 1)
                t = (gaT, gbT)[j]
                nc.scalar.activation(t[:, c, :], B[3 + j][:], ACT.Sigmoid).then_inc(gate_done, 1)

            def gate_tile(c, s, la, lb_, next_hi):
                hi(unit_g(c, 1), 1, G_SLOT[1], s, lb_)
                gate_out(c, 0)
                next_hi()
                gate_out(c, 1)

            gl = L + C
            with act.Fori(0, C - 1) as cp:
                gate_tile(2 * cp, 0, cp + L + 1, cp + gl + 1,
                          lambda: hi(unit_g(2 * cp + 1, 0), 0, G_SLOT[0], 1, cp + L + 1))
                gate_tile(2 * cp + 1, 1, cp + L + 1, cp + gl + 1,
                          lambda: hi(unit_g(2 * cp + 2, 0), 0, G_SLOT[0], 0, cp + L + 2))
            gate_tile(KT - 2, 0, L + C, gl + C, lambda: hi(unit_g(KT - 1, 0), 0, G_SLOT[0], 1, L + C))
            gate_tile(KT - 1, 1, L + C, gl + C, lambda: None)

            for i in range(4):
                act.wait_ge(keys_tr, i + 1)
                if i == 0:
                    act.wait_ge(keys_tr, 4)
                nc.scalar.activation(keysT[:, 4 * i:4 * i + 4, :].rearrange("p a k -> p (a k)"), B[i][:],
                                     ACT.Copy).then_inc(keys_done, 1)

            def rstd_of(b):
                act.wait_ge(ln_var, b + 1)
                nc.scalar.activation(rstd[:, 0:1], mean_var[:, 1:2], ACT.Ln, bias=eps_ln[:, 0:1]).then_inc(ln_rstd, 1)
                act.wait_ge(ln_rstd, 2 * b + 1)
                nc.scalar.activation(rstd[:, 1:2], rstd[:, 0:1], ACT.Exp, scale=-0.5).then_inc(ln_rstd, 1)

            def turn_out(pc, b):
                for kh in range(2):
                    r = use_turn(pc, b, kh)
                    act.wait_ge(t_done, r + 1)
                    nc.scalar.activation(oT[:, 4 * kh:4 * kh + 4, b * P:(b + 1) * P],
                                         B[4 + r % 4][:].rearrange("p (k t) -> p k t", t=P),
                                         ACT.Copy).then_inc(t_act, 1)

            def query_out(pc, h, parts=range(4)):
                bs = blocks(pc)
                n = P * len(bs)
                for i in parts:
                    r = use_query(pc, h, i)
                    act.wait_ge(t_done, r + 1)
                    if i < 2:
                        o = qhT[pc][:, i, 0:n]
                        src = B[4 + r % 4][:, 0:n]
                    else:
                        o = scores[:, bs[0]:bs[0] + len(bs), h, i - 2, :]
                        src = B[4 + r % 4][:, 0:n].rearrange("p (b k) -> p b k", k=NK)
                    nc.scalar.activation(o, src, ACT.Copy).then_inc(t_act, 1)

            def stage_scores(i, bh):
                if not (isinstance(i, int) and i < 1):
                    act.wait_ge(idx_done, i)
                if isinstance(i, int) and i < 2 * PKH:
                    act.wait_ge(*t_reader(use_query(i // PKH, i % PKH, 3)))
                else:
                    act.wait_ge(*t_reader(t_base(2) - 1))
                nc.scalar.activation(stage[:].rearrange("p a k -> p (a k)"), bh, ACT.Copy).then_inc(staged, 1)

            sc_items = scores[:].rearrange("p b h a k -> p (b h) (a k)")

            def exps_of(i):
                act.wait_ge(tk, TK * i + TK_DIFF)
                if not (isinstance(i, int) and i < 1):
                    act.wait_ge(weight_done, i)
                nc.scalar.activation(top_e[:], top_e[:], ACT.Exp, accum_out=e_sum[:, 0:1]).then_inc(exp_done, 1)

            def x_current(b):
                if not (isinstance(b, int) and b < 1):
                    act.wait_ge(u_used, TOPK * PKH * b)
                for i in range(2):
                    nc.scalar.activation(B[2 + i][:], x_sb[:, bass.ds(b, 1), i * 512:(i + 1) * 512].rearrange("p a d -> p (a d)"),
                                         ACT.Copy).then_inc(x1_cur, 1)

            def gelu_of(g, s):
                act.wait_ge(u_used, TOPK * g + TOPK)
                if not (isinstance(g, int) and g < 1):
                    act.wait_ge(coef_done, g)
                nc.scalar.activation(gelu[:], dots[:, s, :], ACT.Gelu).then_inc(gelu_done, 1)

            def make_diag(g, j):
                if j == 0:
                    act.wait_ge(coef_done, g + 1)
                if by_vector(g, j):
                    return
                n = v_row(g, j)
                if not (isinstance(n, int) and n < DR):
                    act.wait_ge(v_used, n - DR + 1)
                nc.scalar.activation(diag[:, diag_slot(g, j), :], ident[:], ACT.Copy, scale=coef[:, j:j + 1]).then_inc(diag_done, 1)

            def item(i, s, tail_h=None, start=None, last=False, finish=None):
                if start is not None:
                    x_current(start)
                if not (isinstance(i, int) and i < 1):
                    gelu_of(i - 1, 1 - s)
                for j in range(TOPK):
                    if not (isinstance(i, int) and i < 1):
                        make_diag(i - 1, j)
                    if j == (3 if finish is None else 5) and not last and not (isinstance(i, int) and i == 0):
                        exps_of(i + 1)
                    if j == 2 and finish is not None:
                        fin_p(finish)
                        fin_rstd(finish)
                    if finish is not None:
                        fin_steps(finish, j)
                    if tail_h is not None:
                        tail_jobs(tail_h, j)
                    if j == 10 and not (last or (isinstance(i, int) and i >= ITEMS - 2)):
                        stage_scores(i + 2, sc_items[:, bass.ds(i + 2, 1), :].rearrange("p a k -> p (a k)"))

            def tail_jobs(h, j):
                for k in jobs(NORM_AT, h, j, 1):
                    rstd_of(1 + k)
                for k in jobs(TURN_AT, h, j, EVAC):
                    turn_out(1, 1 + k)
                for k in jobs(QUERY_AT, h, j, EVAC):
                    query_out(1, k // 2, [k % 2])
                for k in jobs(SCORE_AT, h, j, EVAC):
                    query_out(1, k, [2, 3])

            def fin_p(b):
                act.wait_ge(p_tr, b + 1)
                nc.scalar.activation(pT[:].rearrange("p k t -> p (k t)"), B[6][:, 0:PLE], ACT.Copy).then_inc(pT_done, 1)

            def fin_rstd(b):
                act.wait_ge(x2_var, b + 1)
                nc.scalar.activation(rstd[:, 0:1], mean_var[:, 1:2], ACT.Ln, bias=eps_ln[:, 0:1]).then_inc(x2_rstd, 1)
                act.wait_ge(x2_rstd, 2 * b + 1)
                nc.scalar.activation(rstd[:, 1:2], rstd[:, 0:1], ACT.Exp, scale=-0.5).then_inc(x2_rstd, 1)

            def fin_steps(b, j):
                if j == 6:
                    for kh in range(2):
                        act.wait_ge(x2_tr, 2 * b + kh + 1)
                        nc.scalar.activation(x2T[:, 4 * kh:4 * kh + 4, :].rearrange("p k t -> p (k t)"), B[4 + kh][:],
                                             ACT.Copy).then_inc(x2T_done, 1)
                if j in (11, 15):
                    i = (11, 15).index(j)
                    act.wait_ge(g_mm, 2 * b + i + 1)
                    nc.scalar.activation(gate[:, i * 512:(i + 1) * 512], B[4 + i][:], ACT.Sigmoid).then_inc(g_sig, 1)

            rstd_of(0)
            turn_out(0, 0)
            query_out(0, 0)
            stage_scores(0, sc_items[:, 0, :])
            exps_of(0)
            query_out(0, 1)
            stage_scores(1, sc_items[:, 1, :])
            x_current(0)
            for h in range(2, PKH):
                query_out(0, h)
                if h == 4:
                    exps_of(1)
            for h in range(PKH):
                item(h, h % 2, tail_h=h)
            with act.Fori(1, TB - 1) as b:
                item(PKH * b, 0, start=b)
                item(PKH * b + 1, 1, finish=b - 1)
                with act.Fori(1, PKH // 2) as hp:
                    item(PKH * b + 2 * hp, 0)
                    item(PKH * b + 2 * hp + 1, 1)
            i0 = ITEMS - PKH
            item(i0, 0, start=TB - 1)
            item(i0 + 1, 1, finish=TB - 2)
            with act.Fori(1, PKH // 2 - 1) as hp:
                item(i0 + 2 * hp, 0)
                item(i0 + 2 * hp + 1, 1)
            item(ITEMS - 2, 0)
            item(ITEMS - 1, 1, last=True)
            gelu_of(ITEMS - 1, 1)
            for j in range(TOPK):
                make_diag(ITEMS - 1, j)
                if j == 2:
                    fin_p(TB - 1)
            fin_rstd(TB - 1)
            for j in (6, 11, 15):
                fin_steps(TB - 1, j)

        @block.vector
        def _(dve):
            V = nc.vector
            dve.wait_ge(vec_t, 1)
            V.tensor_copy(vecs[:], B[0][:, 0:NV]).then_inc(lb_step, 1)
            dve.wait_ge(lb_step, 1)
            V.tensor_tensor(lb_m[:], lb0, lb1, ALU.max).then_inc(lb_step, 1)
            dve.wait_ge(lb_step, 2)
            V.tensor_tensor(lb_e[:], vecs[:, 0:2 * HEADS].rearrange("p (a h) -> p a h", a=2),
                            lb_m[:].unsqueeze(1).to_broadcast([P, 2, HEADS]), ALU.subtract).then_inc(lb_step, 1)
            dve.wait_ge(lb_step, 4)
            V.tensor_tensor(lb_m[:], lb_e[:, 0], lb_e[:, 1], ALU.add).then_inc(lb_step, 1)
            dve.wait_ge(lb_step, 5)
            V.reciprocal(lb_m[:], lb_m[:]).then_inc(lb_step, 1)
            dve.wait_ge(lb_step, 6)
            V.tensor_tensor(lb[:], lb_e[:, 0], lb_m[:], ALU.mult).then_inc(lb_step, 1)
            dve.wait_ge(lb_step, 7)
            V.tensor_scalar(one_lb[:], lb[:], -1.0, 1.0, ALU.mult, ALU.add).then_inc(lb_step, 1)
            def lo(n, s, slot, half):
                dve.wait_ge(hi_done, n + 1)
                V.tensor_tensor(w_lo[:, s], raw[:, slot, :, half * P:half * P + P],
                                w_hi[:, s].bitcast(F32), ALU.subtract).then_inc(lo_done, 1)

            def og_out(h, s):
                dve.wait_ge(sgo_done, h + 1)
                V.tensor_tensor(og_silu[:, s], B[3][:], sg_og[:], ALU.mult).then_inc(ogs_done, 1)

            def final(h, s):
                dve.wait_ge(rr_done, h + 1)
                V.scalar_tensor_tensor(out=o_norm[:], in0=B[5][:], scalar=vecs[:, bass.ds(2 * HEADS + h, 1)],
                                       in1=rms_r[:], op0=ALU.mult, op1=ALU.mult).then_inc(on_done, 1)
                dve.wait_ge(on_done, h + 1)
                dve.wait_ge(ogs_done, h + 1)
                V.tensor_tensor(oT[:, h, :], o_norm[:], og_silu[:, s], ALU.mult).then_inc(oT_done, 1)

            def mask(g):
                wait_apart(dve, a_done, g + 1)
                V.copy_predicated(att[:], causal[:].bitcast(U32).unsqueeze(1).to_broadcast([P, TB, P]),
                                  B[4][:].rearrange("p (b i) -> p b i", b=TB)).then_inc(att_done, 1)

            def cumulate(h):
                dve.wait_ge(lnf_done, h + 1)
                V.tensor_tensor_scan(bcum[:], chunk_mask[:], log_f[:], 0.0, ALU.mult, ALU.add).then_inc(cum_done, 1)
                dve.wait_ge(cum_done, h + 1)
                bc = bcum[:].rearrange("p (c t) -> p c t", t=CH)
                V.tensor_tensor(tail_e[:].rearrange("p (c t) -> p c t", t=CH), bc,
                                bc[:, :, CH - 1:CH].to_broadcast([P, NCH, CH]), ALU.subtract).then_inc(dif_done, 1)

            def qk(h, s):
                one = one_lb[:, bass.ds(h, 1)]
                dve.wait_ge(en_done, h + 1)
                V.scalar_tensor_tensor(out=ke[:, s], in0=sg_neg[:], scalar=one, in1=e_neg[:],
                                       op0=ALU.mult, op1=ALU.mult).then_inc(ke_done, 1)
                dve.wait_ge(unit_done, unit_a(h, 1) + 1)
                V.scalar_tensor_tensor(out=qe[:, s], in0=B[1][:], scalar=float(P) ** -0.5, in1=e_pos[:, s],
                                       op0=ALU.mult, op1=ALU.mult).then_inc(qe_done, 1)
                dve.wait_ge(et_done, h + 1)
                V.scalar_tensor_tensor(out=kend[:, s], in0=sg_neg[:], scalar=one, in1=tail_e[:],
                                       op0=ALU.mult, op1=ALU.mult).then_inc(kend_done, 1)

            def states(g, s):
                dve.wait_ge(ds_done, g + 1)
                V.tensor_copy(state[:, 0], B[6][:, 0:P]).then_inc(st_done, 1)
                for c in range(1, NCH - 1):
                    dve.wait_ge(st_done, (NCH - 1) * g + c)
                    V.scalar_tensor_tensor(out=state[:, c], in0=state[:, c - 1],
                                           scalar=e_pos[:, s, c * CH + CH - 1:c * CH + CH],
                                           in1=B[6 + c // 4][:, (c % 4) * P:(c % 4 + 1) * P],
                                           op0=ALU.mult, op1=ALU.add).then_inc(st_done, 1)

            def head(h, s, next_lo):
                first = isinstance(h, int)
                lo(unit_a(h, 1), 1, 1, s)
                if not (first and h < 1):
                    og_out(h - 1, 1 - s)
                if not (first and h < 2):
                    final(h - 2, s)
                if not (first and h < 1):
                    mask(h - 1)
                lo(unit_a(h, 2), 0, 2, s)
                cumulate(h)
                lo(unit_a(h, 3), 1, 3, s)
                qk(h, s)
                if not (first and h < 1):
                    states(h - 1, 1 - s)
                next_lo()

            for k in range(KT):
                dve.wait_ge(xh_done, k + 1)
                V.tensor_tensor(xTl[:, k, :], B[k][:], xTh[:, k, :].bitcast(F32), ALU.subtract).then_inc(xl_done, 1)
                if k == KT // 2 - 1:
                    lo(0, 0, 0, 0)
            head(0, 0, lambda: lo(unit_a(1, 0), 0, 0, 1))
            head(1, 1, lambda: lo(unit_a(2, 0), 0, 0, 0))
            with dve.Fori(1, HEADS // 2) as hp:
                head(2 * hp, 0, lambda: lo(unit_a(2 * hp + 1, 0), 0, 0, 1))
                head(2 * hp + 1, 1, lambda: lo(unit_a(2 * hp + 2, 0), 0, 0, 0))

            def conv_tile(c, s, next_lo):
                int_c = isinstance(c, int)
                lo(unit_c(c, 1), (s + 1) % 2, 1, s)
                if int_c and c == 0:
                    og_out(HEADS - 1, 1)
                    final(HEADS - 2, 0)
                    mask(HEADS - 1)
                lo(unit_c(c, 2), s, 2, s)
                next_lo()
                if int_c and c == 1:
                    final(HEADS - 1, 1)
                if int_c and c == 0:
                    states(HEADS - 1, 1)
                v0 = 3 * HEADS

                def w(j):
                    return vecs[:, bass.ds(v0 + j * KT + c, 1)]

                dve.wait_ge(ch_done, c + 1)
                dve.wait_ge(unit_done, unit_c(c, 1) + 1)
                V.tensor_tensor(u_pad[:, 2:], B[1][:], ch_sb[:], ALU.mult).then_inc(cv_step, 1)
                dve.wait_ge(cv_step, 4 * c + 1)
                V.tensor_scalar(y_a[:], u_pad[:, 2:], w(2), w(3), ALU.mult, ALU.add).then_inc(cv_step, 1)
                dve.wait_ge(cv_step, 4 * c + 2)
                V.scalar_tensor_tensor(out=y_b[:], in0=u_pad[:, 1:SEQ + 1], scalar=w(1), in1=y_a[:],
                                       op0=ALU.mult, op1=ALU.add).then_inc(cv_step, 1)
                dve.wait_ge(cv_step, 4 * c + 3)
                V.scalar_tensor_tensor(out=y_a[:], in0=u_pad[:, 0:SEQ], scalar=w(0), in1=y_b[:],
                                       op0=ALU.mult, op1=ALU.add).then_inc(cv_step, 1)
                dve.wait_ge(cv_step, 4 * c + 4)
                dve.wait_ge(unit_done, unit_c(c, 2) + 1)
                V.tensor_tensor(ycT[:, c, :], y_a[:], B[2][:], ALU.mult).then_inc(yc_done, 1)

            conv_tile(0, 0, lambda: lo(unit_c(1, 0), 1, 0, 1))
            conv_tile(1, 1, lambda: lo(unit_c(2, 0), 0, 0, 0))
            with dve.Fori(1, KT // 2 - 1) as cp:
                conv_tile(2 * cp, 0, lambda: lo(unit_c(2 * cp + 1, 0), 1, 0, 1))
                conv_tile(2 * cp + 1, 1, lambda: lo(unit_c(2 * cp + 2, 0), 0, 0, 0))
            conv_tile(KT - 2, 0, lambda: lo(unit_c(KT - 1, 0), 1, 0, 1))
            conv_tile(KT - 1, 1, lambda: lo(unit_g(0, 0), 0, G_SLOT[0], 0))
            with dve.Fori(0, KT // 2 - 1) as cp:
                lo(unit_g(2 * cp, 1), 1, G_SLOT[1], 0)
                lo(unit_g(2 * cp + 1, 0), 0, G_SLOT[0], 1)
                lo(unit_g(2 * cp + 1, 1), 1, G_SLOT[1], 1)
                lo(unit_g(2 * cp + 2, 0), 0, G_SLOT[0], 0)
            lo(unit_g(KT - 2, 1), 1, G_SLOT[1], 0)
            lo(unit_g(KT - 1, 0), 0, G_SLOT[0], 1)
            lo(unit_g(KT - 1, 1), 1, G_SLOT[1], 1)

            def merge(pc, c, parts=range(4)):
                bs = blocks(pc)
                t = slice(bs[0] * P, (bs[-1] + 1) * P)
                n = P * len(bs)
                for i in parts:
                    r = use_merge(pc, c, i)
                    g = (gaT, gbT)[i // 2][:, 2 * c + i % 2, t]
                    dve.wait_ge(t_done, r + 1)
                    if i == 0 and c == 0 and pc == 0:
                        dve.wait_ge(gate_done, 2 * KT)
                    V.tensor_tensor(g, g, B[4 + r % 4][:, 0:n], ALU.mult).then_inc(t_dve, 1)
                    if i >= 2:
                        k = 2 * c + i - 2
                        dve.wait_ge(*t_reader(r))
                        V.tensor_tensor(gaT[:, k, t], gaT[:, k, t], gbT[:, k, t], ALU.add).then_inc(merged, 1)

            def residual(pc, c, b):
                r = use_out(pc, c, b)
                dve.wait_ge(t_done, r + 1)
                xs = x_sb[:, b, c * CW:(c + 1) * CW]
                V.scalar_tensor_tensor(out=xs, in0=xs, scalar=ALPHA, in1=B[4 + r % 4][:, 0:CW],
                                       op0=ALU.mult, op1=ALU.add).then_inc(t_dve, 1)

            def norm(n, src, dst, gb, step, var, rst, done):
                for i in range(2):
                    V.bn_stats(stats[:, i, :], src[:, i * 512:(i + 1) * 512]).then_inc(step, 1)
                wait_apart(dve, step, 4 * n + 2)
                V.bn_aggr(mean_var[:], stats[:].rearrange("p a s -> p (a s)")).then_inc(var, 1)
                dve.wait_ge(rst, 2 * n + 2)
                V.tensor_scalar(dst, src, mean_var[:, 0:1], rstd[:, 1:2], ALU.subtract, ALU.mult).then_inc(step, 1)
                dve.wait_ge(step, 4 * n + 3)
                V.tensor_tensor(dst, dst, gb[:, 0, :], ALU.mult).then_inc(step, 1)
                dve.wait_ge(step, 4 * n + 4)
                V.tensor_tensor(dst, dst, gb[:, 1, :], ALU.add).then_inc(done, 1)

            def norm1(pc, b):
                dve.wait_ge(*t_reader(use_out(pc, 3, b)))
                if b == 0:
                    dve.wait_ge(ln1_in, 32)
                norm(b, x_sb[:, b, :], x_sb[:, b, :], ln1, ln_step, ln_var, ln_rstd, x1_done)

            LOWEST = float(np.finfo(np.float32).min)

            def row(t, k):
                return t.unsqueeze(2).to_broadcast([P, TOPK, k])

            def col(t, k):
                return t.unsqueeze(1).to_broadcast([P, k, TOPK])

            def search(i, s):
                base = TK * i
                hot_hi = hot[:].rearrange("p (a b) -> p a b", b=TOPK)
                hot_lo = stage[:].rearrange("p a k -> p (a k)").rearrange("p (a b) -> p a b", b=TOPK)
                wait_apart(dve, staged, i + 1)
                for a in range(2):
                    V.max(best[:, a, 0:8], stage[:, a]).then_inc(tk, 1)
                for a in range(2):
                    wait_apart(dve, tk, base + 1 + a)
                    V.max_index(best_i[:, a, 0:8], best[:, a, 0:8], stage[:, a]).then_inc(tk, 1)
                for a in range(2):
                    wait_apart(dve, tk, base + 3 + a)
                    V.match_replace(stage[:, a], best[:, a, 0:8], stage[:, a], LOWEST).then_inc(tk, 1)
                for a in range(2):
                    wait_apart(dve, tk, base + 5 + a)
                    V.max(best[:, a, 8:16], stage[:, a]).then_inc(tk, 1)
                for a in range(2):
                    wait_apart(dve, tk, base + 7 + a)
                    V.max_index(best_i[:, a, 8:16], best[:, a, 8:16], stage[:, a]).then_inc(tk, 1)
                dve.wait_ge(tk, base + 8)
                V.tensor_tensor(cand[:].rearrange("p (a b) -> p a b", b=TOPK), row(best[:, 0], TOPK),
                                col(best[:, 1], TOPK), ALU.add).then_inc(tk, 1)
                wait_apart(dve, tk, base + 11)
                V.max(top[:, 0:8], cand[:]).then_inc(tk, 1)
                wait_apart(dve, tk, base + 12)
                V.max_index(pos[:, 0:8], top[:, 0:8], cand[:]).then_inc(tk, 1)
                wait_apart(dve, tk, base + 13)
                V.match_replace(cand[:], top[:, 0:8], cand[:], LOWEST).then_inc(tk, 1)
                wait_apart(dve, tk, base + 14)
                V.max(top[:, 8:16], cand[:]).then_inc(tk, 1)
                wait_apart(dve, tk, base + 15)
                V.max_index(pos[:, 8:16], top[:, 8:16], cand[:]).then_inc(tk, 1)
                V.tensor_scalar(top_e[:], top[:], top[:, 0:1], None, ALU.subtract).then_inc(tk, 1)
                dve.wait_ge(tk, base + 16)
                V.tensor_scalar(pos_hi[:], pos[:], 4, None, ALU.logical_shift_right).then_inc(tk, 1)
                V.tensor_scalar(pos_lo[:], pos[:], TOPK - 1, None, ALU.bitwise_and).then_inc(tk, 1)
                dve.wait_ge(tk, base + 18)
                V.tensor_tensor(hot_hi, row(pos_hi[:], TOPK), col(iota16[:], TOPK), ALU.is_equal).then_inc(tk, 1)
                dve.wait_ge(tk, base + 19)
                V.tensor_tensor(hot_lo, row(pos_lo[:], TOPK), col(iota16[:], TOPK), ALU.is_equal).then_inc(tk, 1)
                dve.wait_ge(tk, base + 20)
                V.tensor_tensor(hot_hi, hot_hi, col(best_i[:, 0], TOPK), ALU.mult).then_inc(tk, 1)
                dve.wait_ge(tk, base + 21)
                V.tensor_tensor(hot_lo, hot_lo, col(best_i[:, 1], TOPK), ALU.mult).then_inc(tk, 1)
                dve.wait_ge(tk, base + 22)
                V.reduce_sum(sel[:, 0], hot_hi, AX_X).then_inc(tk, 1)
                dve.wait_ge(tk, base + 23)
                V.reduce_sum(sel[:, 1], hot_lo, AX_X).then_inc(tk, 1)
                dve.wait_ge(tk, base + 25)
                if not (isinstance(i, int) and i < 2):
                    dve.wait_ge(idxv_done, i - 1)
                V.scalar_tensor_tensor(out=idx[:, s], in0=sel[:, 0], scalar=float(NK), in1=sel[:, 1],
                                       op0=ALU.mult, op1=ALU.add).then_inc(idx_done, 1)

            def weights(i, s):
                dve.wait_ge(exp_done, i + 1)
                V.reciprocal(e_rec[:], e_sum[:]).then_inc(rec_done, 1)
                dve.wait_ge(rec_done, i + 1)
                V.tensor_scalar(weight[:, s], top_e[:], e_rec[:, 0:1], None, ALU.mult).then_inc(weight_done, 1)

            def coefs(g, s):
                dve.wait_ge(gelu_done, g + 1)
                dve.wait_ge(weight_done, g + 1)
                if not (isinstance(g, int) and g < 1):
                    dve.wait_ge(diag_done, v_row(g, 0))
                    own = [j for j in range(TOPK) if isinstance(g, int) and by_vector(g - 1, j)]
                    if own:
                        dve.wait_ge(*v_reader(g - 1, own[-1]))
                V.tensor_tensor(coef[:], gelu[:], weight[:, s], ALU.mult).then_inc(coef_done, 1)

            def dot(i, s, j):
                dve.wait_ge(u_in[j % UR], 32 * i + 16 * (j // UR) + 16)
                V.tensor_tensor_reduce(u_ring[:, j % UR, :], u_ring[:, j % UR, :], x_cur[:], 1.0, 0.0, ALU.mult,
                                       ALU.add, dots[:, s, j:j + 1]).then_inc(u_used, 1)

            def sum_v(g, j):
                n = SHARED.index((g, j))
                if n > 0:
                    dve.wait_ge(acc_step, n)
                dve.wait_ge(coef_done, g + 1)
                dve.wait_ge(v_in[j % VR], 64 * g + 16 * (j // VR) + 16)
                if n == 0:
                    V.tensor_scalar(acc[:], v_ring[:, j % VR, :], coef[:, j:j + 1], None, ALU.mult).then_inc(acc_step, 1)
                else:
                    V.scalar_tensor_tensor(out=acc[:], in0=v_ring[:, j % VR, :], scalar=coef[:, j:j + 1], in1=acc[:],
                                           op0=ALU.mult, op1=ALU.add).then_inc(acc_step, 1)

            def fin_sum(b):
                dve.wait_ge(v_used, TOPK * PKH * b + TOPK * PKH - SHARED_ROWS)
                if not (isinstance(b, int) and b < 1):
                    dve.wait_ge(stored, 16 * b)
                for i in range(2):
                    d = slice(i * 512, (i + 1) * 512)
                    V.scalar_tensor_tensor(out=x2[:, d], in0=x_sb[:, bass.ds(b, 1), d].rearrange("p a d -> p (a d)"),
                                           scalar=ALPHA, in1=B[i][:], op0=ALU.mult, op1=ALU.add).then_inc(acc_out, 1)

            def fin_norm(b):
                dve.wait_ge(acc_out, 2 * b + 2)
                dve.wait_ge(fin_in, 64)
                norm(b, x2[:], x2[:], ln2, x2_step, x2_var, x2_rstd, x2_done)

            def fin_out(b):
                for i in range(2):
                    d = slice(i * 512, (i + 1) * 512)
                    dve.wait_ge(g_sig, 2 * b + i + 1)
                    dve.wait_ge(p_mm, 2 * b + i + 1)
                    V.tensor_tensor(gate[:, d], gate[:, d], B[6 + i][:], ALU.mult).then_inc(fin_step, 1)
                dve.wait_ge(fin_step, 2 * b + 2)
                V.tensor_tensor(x2[:], x2[:], gate[:], ALU.add).then_inc(x3_done, 1)

            def tail_jobs(h, j):
                for k in jobs(MERGE_AT, h, j, EVAC):
                    merge(1, k // 4, [k % 4])
                for k in jobs(OUT_AT, h, j, EVAC):
                    residual(1, k // (TB - 1), 1 + k % (TB - 1))
                for k in jobs(NORM_AT, h, j):
                    norm1(1, 1 + k)

            def item(i, s, tail_h=None, start=None, last=False, finish=None):
                if start is not None:
                    dve.wait_ge(x1_cur, 2 * start + 2)
                if not (isinstance(i, int) and i < 1):
                    coefs(i - 1, 1 - s)
                if finish is not None:
                    fin_sum(finish)
                for j in range(TOPK):
                    dot(i, s, j)
                    if j == 1 and finish is not None:
                        fin_norm(finish)
                    if j == (1 if finish is None else 4) and not last and not (isinstance(i, int) and i == 0):
                        search(i + 1, 1 - s)
                    if j == (6 if finish is None else 8) and not last:
                        weights(i + 1, 1 - s)
                    if isinstance(i, int) and j >= 2 and by_vector(i - 1, j - 2):
                        sum_v(i - 1, j - 2)
                    if isinstance(i, int) and j == TOPK - 1 and by_vector(i - 1, j):
                        sum_v(i - 1, j)
                    if tail_h is not None:
                        tail_jobs(tail_h, j)
                if finish is not None:
                    fin_out(finish)

            for c in range(4):
                merge(0, c)
            for c in range(4):
                residual(0, c, 0)
            norm1(0, 0)
            search(0, 0)
            weights(0, 0)
            search(1, 1)
            for h in range(PKH):
                item(h, h % 2, tail_h=h, start=0 if h == 0 else None)
            with dve.Fori(1, TB - 1) as b:
                item(PKH * b, 0, start=b)
                item(PKH * b + 1, 1, finish=b - 1)
                with dve.Fori(1, PKH // 2) as hp:
                    item(PKH * b + 2 * hp, 0)
                    item(PKH * b + 2 * hp + 1, 1)
            i0 = ITEMS - PKH
            item(i0, 0, start=TB - 1)
            item(i0 + 1, 1, finish=TB - 2)
            with dve.Fori(1, PKH // 2 - 1) as hp:
                item(i0 + 2 * hp, 0)
                item(i0 + 2 * hp + 1, 1)
            item(ITEMS - 2, 0)
            item(ITEMS - 1, 1, last=True)
            coefs(ITEMS - 1, 1)
            fin_sum(TB - 1)
            fin_norm(TB - 1)
            fin_out(TB - 1)

        @block.tensor
        def _(pe):
            T = nc.tensor
            pe.wait_ge(consts, CONSTS)
            pe.wait_ge(vecs_in, 64)
            T.transpose(B[0][:, 0:NV], vec_rows[0:NV, :], ident[0:NV, 0:NV]).then_inc(vec_t, 1)
            pe.wait_ge(lb_step, 1)
            for b in range(TB):
                pe.wait_ge(x_in[b], 16)
                for k in range(KT):
                    last = T.transpose(B[k][:, b * P:(b + 1) * P], x_sb[:, b, k * P:(k + 1) * P], ident[:])
                    if b == TB - 1:
                        last.then_inc(x_tr, 1)

            def unit(n, s, bk):
                pe.wait_ge(lo_done, n + 1)
                for k in range(KT):
                    if isinstance(n, int) and n < 2:
                        pe.wait_ge(xl_done, max(k, n) + 1)
                    for i, (w, xx) in enumerate(((w_hi, xTh), (w_lo, xTh), (w_hi, xTl))):
                        last = T.matmul(B[bk][:], w[:, s, k, :], xx[:, k, :], start=(k == 0 and i == 0),
                                        stop=(k == KT - 1 and i == 2))
                last.then_inc(unit_done, 1)

            def turn(g, s):
                pe.wait_ge(vT_done, g + 1)
                if not (isinstance(g, int) and g < 1):
                    pe.wait_ge(st_done, (NCH - 1) * g)
                for b in range(TB):
                    last = T.transpose(B[6][:, b * P:(b + 1) * P], vT_sb[:, b * P:(b + 1) * P], ident[:])
                last.then_inc(vtr_done, 1)
                pe.wait_ge(kend_done, g + 1)
                for b in range(TB):
                    last = T.transpose(B[7][:, b * P:(b + 1) * P], kend[:, s, b * P:(b + 1) * P], ident[:])
                last.then_inc(ktr_done, 1)
                pe.wait_ge(ke_done, g + 1)
                pe.wait_ge(qe_done, g + 1)
                if not (isinstance(g, int) and g < 1):
                    pe.wait_ge(rln_done, g)
                for b in range(TB):
                    t = slice(b * P, (b + 1) * P)
                    last = T.matmul(B[4][:, t], ke[:, s, t], qe[:, s, t], start=True, stop=True)
                last.then_inc(a_done, 1)

            def intra(g):
                pe.wait_ge(att_done, g + 1)
                pe.wait_ge(vtok_done, g + 1)
                if not (isinstance(g, int) and g < 1):
                    pe.wait_ge(on_done, g)
                for b in range(TB):
                    T.matmul(B[5][:, b * P:(b + 1) * P], v_tok[:, b, :], att[:, b, :], start=(b == 0),
                             stop=False, skip_group_check=True)
                pe.wait_ge(ktok_done, 2 * g + 2)
                for c in range(NCH - 1):
                    kk = (k_even, k_odd)[c % 2]
                    last = T.matmul(B[6 + c // 4][:, (c % 4) * P:(c % 4 + 1) * P], kk[:, c // 2, :],
                                    v_tok[:, c // 2, :], start=True, stop=True, skip_group_check=True)
                last.then_inc(ds_done, 1)

            def inter(g, s):
                pe.wait_ge(st_done, (NCH - 1) * g + NCH - 1)
                for c in range(1, NCH):
                    t = slice(c * CH, (c + 1) * CH)
                    last = T.matmul(B[5][:, t], state[:, c - 1], qe[:, s, t], start=False, stop=(c == NCH - 1),
                                    skip_group_check=True)
                last.then_inc(o_done, 1)

            def mean_square(g):
                pe.wait_ge(sq_done, g + 1)
                T.matmul(B[4][:], ones[:], o_sq[:], start=True, stop=True).then_inc(rms_done, 1)

            def head(h, s):
                int_h = isinstance(h, int)
                prev = not (int_h and h < 1)
                if prev:
                    pe.wait_ge(f_sig, 2 * h)
                unit(unit_a(h, 0), 0, 0)
                if prev:
                    turn(h - 1, 1 - s)
                    pe.wait_ge(qe_done, h)
                unit(unit_a(h, 1), 1, 1)
                if prev:
                    intra(h - 1)
                    pe.wait_ge(vT_done, h)
                unit(unit_a(h, 2), 0, 2)
                if prev:
                    inter(h - 1, 1 - s)
                    pe.wait_ge(ogs_done, h)
                unit(unit_a(h, 3), 1, 3)
                if prev:
                    mean_square(h - 1)

            head(0, 0)
            head(1, 1)
            with pe.Fori(1, HEADS // 2) as hp:
                head(2 * hp, 0)
                head(2 * hp + 1, 1)

            def conv_tile(c, s):
                int_c = isinstance(c, int)
                if int_c and c == 0:
                    pe.wait_ge(f_sig, 2 * HEADS)
                    unit(unit_c(c, 0), s, 0)
                    turn(HEADS - 1, 1)
                    pe.wait_ge(qe_done, HEADS)
                    unit(unit_c(c, 1), 1 - s, 1)
                    intra(HEADS - 1)
                    pe.wait_ge(vT_done, HEADS)
                    unit(unit_c(c, 2), s, 2)
                    inter(HEADS - 1, 1)
                    return
                pe.wait_ge(ch_done, c)
                unit(unit_c(c, 0), s, 0)
                if int_c and c == 1:
                    mean_square(HEADS - 1)
                pe.wait_ge(cv_step, 4 * c - 3)
                unit(unit_c(c, 1), 1 - s, 1)
                pe.wait_ge(yc_done, c)
                unit(unit_c(c, 2), s, 2)

            conv_tile(0, 0)
            conv_tile(1, 1)
            with pe.Fori(1, KT // 2) as cp:
                conv_tile(2 * cp, 0)
                conv_tile(2 * cp + 1, 1)

            def gate_tile(c, i):
                if isinstance(c, int) and c == 0:
                    pe.wait_ge(ogs_done, HEADS)
                    pe.wait_ge(rln_done, HEADS)
                else:
                    pe.wait_ge(gate_done, 2 * c - 1)
                unit(unit_g(c, 0), 0, 3)
                if not (isinstance(c, int) and c == 0):
                    pe.wait_ge(gate_done, 2 * c)
                unit(unit_g(c, 1), 1, 4)

            gate_tile(0, 0)
            with pe.Fori(1, KT) as c:
                gate_tile(c, 0)

            pe.wait_ge(keys_in, 16)
            pe.wait_ge(gate_done, 2 * KT)
            for i in range(4):
                for a in range(4):
                    last = T.transpose(B[i][:, a * P:(a + 1) * P], keysT[:, 4 * i + a, :], ident[:])
                last.then_inc(keys_tr, 1)

            def t_free(r):
                if r >= 4:
                    pe.wait_ge(*t_reader(r - 4))

            def merge(pc, c, parts=range(4)):
                bs = blocks(pc)
                t = slice(bs[0] * P, (bs[-1] + 1) * P)
                n = P * len(bs)
                for i in parts:
                    ab, half = i // 2, i % 2
                    _, slot, loads = t_chunk(pc, 2 * c + ab)
                    pe.wait_ge(raw_in[slot], 16 * loads)
                    if pc == 0 and c == 0:
                        pe.wait_ge((oT_done, yc_done)[ab], KT)
                    r = use_merge(pc, c, i)
                    t_free(r)
                    for k in range(KT):
                        last = T.matmul(B[4 + r % 4][:, 0:n], raw[:, slot, k, half * P:half * P + P],
                                        (oT, ycT)[ab][:, k, t], start=(k == 0), stop=(k == KT - 1))
                    last.then_inc(t_done, 1)

            def out_chunk(pc, c, b):
                _, slot, loads = t_chunk(pc, 8 + c)
                pe.wait_ge(raw_in[slot], 16 * loads)
                pe.wait_ge(merged, KT * pc + KT)
                r = use_out(pc, c, b)
                t_free(r)
                for k in range(KT):
                    last = T.matmul(B[4 + r % 4][:, 0:CW], gaT[:, k, b * P:(b + 1) * P], raw[:, slot, k, :],
                                    start=(k == 0), stop=(k == KT - 1))
                last.then_inc(t_done, 1)

            def turn_x(pc, b):
                pe.wait_ge(x1_done, b + 1)
                for kh in range(2):
                    r = use_turn(pc, b, kh)
                    t_free(r)
                    for k in range(4):
                        last = T.transpose(B[4 + r % 4][:, k * P:(k + 1) * P],
                                           x_sb[:, b, (4 * kh + k) * P:(4 * kh + k + 1) * P], ident[:])
                    last.then_inc(t_done, 1)

            def query(pc, h, parts=range(4)):
                bs = blocks(pc)
                t = slice(bs[0] * P, (bs[-1] + 1) * P)
                n = P * len(bs)
                _, slot, loads = t_chunk(pc, 12 + h)
                pe.wait_ge(raw_in[slot], 16 * loads)
                if h == 0:
                    pe.wait_ge(*t_reader(use_turn(pc, bs[-1], 1)))
                    pe.wait_ge(keys_done, 4)
                for a in [i for i in parts if i < 2]:
                    r = use_query(pc, h, a)
                    t_free(r)
                    for k in range(KT):
                        last = T.matmul(B[4 + r % 4][:, 0:n], raw[:, slot, k, a * P:a * P + P], oT[:, k, t],
                                        start=(k == 0), stop=(k == KT - 1))
                    last.then_inc(t_done, 1)
                for a in [i - 2 for i in parts if i >= 2]:
                    r = use_query(pc, h, 2 + a)
                    t_free(r)
                    pe.wait_ge(*t_reader(use_query(pc, h, a)))
                    for i in range(len(bs)):
                        last = T.matmul(B[4 + r % 4][:, i * P:(i + 1) * P], qhT[pc][:, a, i * P:(i + 1) * P],
                                        keysT[:, 2 * h + a, :], start=True, stop=True)
                    last.then_inc(t_done, 1)

            def sum_v(g, j, first=False, final=False):
                if by_vector(g, j):
                    return
                pe.wait_ge(v_in[j % VR], 64 * g + 16 * (j // VR) + 16)
                pe.wait_ge(diag_done, v_row(g, j) + 1)
                for i in range(2):
                    last = T.matmul(B[i][:], diag[:, diag_slot(g, j), :], v_ring[:, j % VR, i * 512:(i + 1) * 512],
                                    start=first, stop=final, skip_group_check=True)
                last.then_inc(v_used, 1)

            def fin_steps(b, j):
                if j == 1:
                    pe.wait_ge(*t_reader(t_base(2) - 1))
                    if not (isinstance(b, int) and b < 1):
                        pe.wait_ge(x3_done, b)
                    pe.wait_ge(p_in, 16 * b + 16)
                    for k in range(PLE // P):
                        last = T.transpose(B[6][:, k * P:(k + 1) * P], p_sb[:, k * P:(k + 1) * P], ident[:])
                    last.then_inc(p_tr, 1)
                if j == 3:
                    pe.wait_ge(fin_in, 64)
                    pe.wait_ge(pT_done, b + 1)
                    for i in range(2):
                        for k in range(PLE // P):
                            last = T.matmul(B[6 + i][:], pT[:, k, :], w_ple[:, k, i * 512:(i + 1) * 512],
                                            start=(k == 0), stop=(k == PLE // P - 1))
                        last.then_inc(p_mm, 1)
                if j == 5:
                    pe.wait_ge(x2_done, b + 1)
                    for kh in range(2):
                        for k in range(4):
                            last = T.transpose(B[4 + kh][:, k * P:(k + 1) * P],
                                               x2[:, (4 * kh + k) * P:(4 * kh + k + 1) * P], ident[:])
                        last.then_inc(x2_tr, 1)
                if j in (7, 9, 11, 13):
                    i, k0 = divmod((7, 9, 11, 13).index(j), 2)
                    pe.wait_ge(x2T_done, 2 * b + 2)
                    for k in range(k0 * KT // 2, (k0 + 1) * KT // 2):
                        last = T.matmul(B[4 + i][:], x2T[:, k, :], w_gate[:, k, i * 512:(i + 1) * 512],
                                        start=(k == 0), stop=(k == KT - 1), skip_group_check=True)
                    if k0 == 1:
                        last.then_inc(g_mm, 1)

            def tail_jobs(h, j):
                for k in jobs(MERGE_AT, h, j):
                    merge(1, k // 4, [k % 4])
                for k in jobs(OUT_AT, h, j):
                    out_chunk(1, k // (TB - 1), 1 + k % (TB - 1))
                for k in jobs(TURN_AT, h, j):
                    turn_x(1, 1 + k)
                for k in jobs(QUERY_AT, h, j):
                    query(1, k // 2, [k % 2])
                for k in jobs(SCORE_AT, h, j):
                    query(1, k, [2, 3])

            def item(i, s, tail_h=None, finish=None, first=False, final=False, add_acc=False):
                if finish is not None:
                    pe.wait_ge(acc_out, 2 * finish + 2)
                for j in range(TOPK):
                    if not (isinstance(i, int) and i < 1):
                        sum_v(i - 1, j, first and j == 0, final and j == TOPK - 1)
                    if add_acc and j == TOPK - 2:
                        pe.wait_ge(acc_step, SHARED_ROWS)
                        for a in range(2):
                            T.matmul(B[a][:], ident[:], acc[:, a * 512:(a + 1) * 512], start=False, stop=False,
                                     skip_group_check=True)
                    if finish is not None:
                        fin_steps(finish, j)
                    if tail_h is not None:
                        tail_jobs(tail_h, j)

            for c in range(4):
                merge(0, c)
            for c in range(4):
                out_chunk(0, c, 0)
            turn_x(0, 0)
            for h in range(PKH):
                query(0, h)
            for h in range(PKH):
                item(h, h % 2, tail_h=h, first=(h == 1), add_acc=(h == PKH - 1))
            with pe.Fori(1, TB) as b:
                item(PKH * b, 0, final=True)
                item(PKH * b + 1, 1, finish=b - 1, first=True)
                with pe.Fori(1, PKH // 2) as hp:
                    item(PKH * b + 2 * hp, 0)
                    item(PKH * b + 2 * hp + 1, 1)
            for j in range(TOPK):
                sum_v(ITEMS - 1, j, final=(j == TOPK - 1))
                if j in (1, 3):
                    fin_steps(TB - 1, j)
            for j in (5, 7, 9, 11, 13):
                fin_steps(TB - 1, j)


_INS = ["x", "p", "w_in", "lb_param", "hg_norm_g", "conv_w", "conv_b", "w_branch_a", "w_branch_b", "w_out",
        "ln1_g", "ln1_b", "pk_w_q", "pk_sub_keys", "pk_u", "pk_v", "ln2_g", "ln2_b", "ple_w_gate", "ple_w_proj"]


def kernel(**inputs):
    import numpy as _np
    import concourse.bacc as _bacc
    from concourse import mybir as _mybir
    from concourse.bass_utils import run_bass_kernel_spmd as _run

    nc = _bacc.Bacc("TRN2", target_bir_lowering=False, num_devices=1)
    arrays, args = {}, []
    for name in _INS:
        a = _np.ascontiguousarray(inputs[name])
        arrays[f"in_{name}"] = a
        args.append(nc.dram_tensor(f"in_{name}", a.shape, _mybir.dt.from_np(a.dtype), kind="ExternalInput").ap())
    out = nc.dram_tensor("out_x", inputs["x"].shape, F32, kind="ExternalOutput").ap()
    build(nc, *args, out)
    r = _run(nc, [arrays], core_ids=[0])
    return r.results[0]["out_x"]
```
